# Optimizing a Trainium2 kernel written in Bass

```python
import math
import jax, jax.numpy as jnp
from jax import lax
import numpy as np

D_MODEL = 1024
BATCH = 1
SEQ = 256
DEPTH = 1

HEAD_DIM = 128
H_DELTA = D_MODEL // HEAD_DIM
DK_DELTA = HEAD_DIM
DV_DELTA = HEAD_DIM
CONV_WIDTH = 4
CHUNK = 64
H_DIFF = D_MODEL // HEAD_DIM
DH_DIFF = HEAD_DIM // 2
DV_DIFF = HEAD_DIM
Q_BLOCK = 128
N_BUCKETS = 32
MAX_DISTANCE = 128
N_EXPERTS = 32
TOP_K = 4
D_FF = D_MODEL
SWIGLU_LIMIT = 7.0
SWIGLU_ALPHA = 1.702
EXPERT_BLOCK = 256
EPS = 1e-6

W_DELTA_QK = H_DELTA * DK_DELTA
W_DELTA_V = H_DELTA * DV_DELTA
W_DIFF_QK = H_DIFF * 2 * DH_DIFF
W_DIFF_V = H_DIFF * DV_DIFF
CONV_CH = 2 * W_DELTA_QK + W_DELTA_V
IN_SPLITS = (W_DELTA_QK, W_DELTA_QK, W_DELTA_V, W_DELTA_V, H_DELTA, H_DELTA,
             W_DIFF_QK, W_DIFF_QK, W_DIFF_V, D_MODEL, D_MODEL)
D_IN = sum(IN_SPLITS)

kernel_name = 'hybrid_gdn_diffattn_moe_block'

def rms_norm(x, gain):
    xf = x.astype(jnp.float32)
    y = xf * lax.rsqrt(jnp.mean(xf * xf, axis=-1, keepdims=True) + EPS)
    return (y * gain.astype(jnp.float32)).astype(x.dtype)

def l2_normalize(x):
    xf = x.astype(jnp.float32)
    return xf * lax.rsqrt(jnp.sum(xf * xf, axis=-1, keepdims=True) + EPS)

def causal_depthwise_conv(x, w):
    k_width, ch = w.shape
    return lax.conv_general_dilated(
        x, w[:, None, :].astype(x.dtype), window_strides=(1,), padding=[(k_width - 1, 0)],
        dimension_numbers=('NWC', 'WIO', 'NWC'), feature_group_count=ch)

def gated_delta_rule(q, k, v, beta, g):
    bsz, seq, nh, dk = q.shape
    dv = v.shape[-1]
    n_chunks = seq // CHUNK

    def chunks(t):
        t = jnp.moveaxis(t.astype(jnp.float32), 2, 1)
        return t.reshape(t.shape[:2] + (n_chunks, CHUNK) + t.shape[3:])

    qc, kc, vc, bc = chunks(q), chunks(k), chunks(v), chunks(beta)
    gc = jnp.cumsum(chunks(g), axis=-1)
    incl = jnp.tril(jnp.ones((CHUNK, CHUNK), bool))
    strict = jnp.tril(jnp.ones((CHUNK, CHUNK), bool), k=-1)
    decay = jnp.exp(jnp.where(incl, gc[..., :, None] - gc[..., None, :], -jnp.inf))
    kb = kc * bc[..., None]
    a_mat = jnp.where(strict, jnp.einsum('bhnid,bhnjd->bhnij', kb, kc) * decay, 0.0)
    eye = jnp.eye(CHUNK, dtype=jnp.float32)
    t_mat = lax.linalg.triangular_solve(eye + a_mat, jnp.broadcast_to(eye, a_mat.shape),
                                        left_side=True, lower=True, unit_diagonal=True)
    u = jnp.einsum('bhnij,bhnje->bhnie', t_mat, vc * bc[..., None])
    w = jnp.einsum('bhnij,bhnjd->bhnid', t_mat, kb * jnp.exp(gc)[..., None])
    qk = jnp.einsum('bhnid,bhnjd->bhnij', qc, kc) * decay
    g_last = gc[..., -1]
    k_to_end = kc * jnp.exp(g_last[..., None] - gc)[..., None]
    q_dec = qc * jnp.exp(gc)[..., None]

    def step(state, xs):
        u_i, w_i, qk_i, q_i, k_i, gl_i = xs
        v_new = u_i - jnp.einsum('bhcd,bhde->bhce', w_i, state)
        o_i = jnp.einsum('bhcd,bhde->bhce', q_i, state) + jnp.einsum('bhij,bhje->bhie', qk_i, v_new)
        state = state * jnp.exp(gl_i)[..., None, None] + jnp.einsum('bhcd,bhce->bhde', k_i, v_new)
        return state, o_i

    xs = tuple(jnp.moveaxis(t, 2, 0) for t in (u, w, qk, q_dec, k_to_end, g_last))
    _, o = lax.scan(step, jnp.zeros((bsz, nh, dk, dv), jnp.float32), xs)
    o = jnp.moveaxis(o, 0, 2).reshape(bsz, nh, seq, dv)
    return jnp.moveaxis(o, 1, 2)

def t5_bucket(rel):
    n = jnp.maximum(-rel, 0)
    max_exact = N_BUCKETS // 2
    nf = jnp.maximum(n, 1).astype(jnp.float32)
    large = max_exact + (jnp.log(nf / max_exact) / math.log(MAX_DISTANCE / max_exact)
                         * (N_BUCKETS - max_exact)).astype(jnp.int32)
    large = jnp.minimum(large, N_BUCKETS - 1)
    return jnp.where(n < max_exact, n, large)

def diff_attention(q, k, v, lam, rel_bias):
    bsz, seq, nh, _, dh = q.shape
    dv = v.shape[-1]
    n_qb = seq // Q_BLOCK
    scale = dh ** -0.5
    qb = jnp.moveaxis(q.reshape(bsz, n_qb, Q_BLOCK, nh, 2, dh), 1, 0)
    k_pos = jnp.arange(seq, dtype=jnp.int32)

    def block(args):
        q_blk, start = args
        q_pos = start + jnp.arange(Q_BLOCK, dtype=jnp.int32)
        rel = k_pos[None, :] - q_pos[:, None]
        bias = jnp.transpose(rel_bias[t5_bucket(rel)], (2, 0, 1)).astype(jnp.float32)
        logits = jnp.einsum('bqhmd,bkhmd->bhmqk', q_blk, k).astype(jnp.float32) * scale
        logits = logits + bias[None, :, None]
        logits = jnp.where(rel[None, None, None] <= 0, logits, -jnp.inf)
        p = jax.nn.softmax(logits, axis=-1)
        attn = p[:, :, 0] - lam * p[:, :, 1]
        return jnp.einsum('bhqk,bkhe->bqhe', attn.astype(v.dtype), v)

    starts = jnp.arange(n_qb, dtype=jnp.int32) * Q_BLOCK
    out = lax.map(block, (qb, starts))
    return jnp.moveaxis(out, 0, 1).reshape(bsz, seq, nh, dv)

def clamped_swiglu(hid):
    glu, lin = hid[..., ::2], hid[..., 1::2]
    glu = jnp.minimum(glu, SWIGLU_LIMIT)
    lin = jnp.clip(lin, -SWIGLU_LIMIT, SWIGLU_LIMIT)
    return glu * jax.nn.sigmoid(SWIGLU_ALPHA * glu) * (lin + 1.0)

def moe_ffn(h, w_router, b_router, w_up, b_up, w_down, b_down):
    n_tok, d = h.shape
    logits = (h @ w_router + b_router).astype(jnp.float32)
    top_val, top_idx = lax.top_k(logits, TOP_K)
    top_w = jax.nn.softmax(top_val, axis=-1)
    n_assign = n_tok * TOP_K
    flat_e = top_idx.reshape(-1).astype(jnp.int32)
    flat_tok = jnp.repeat(jnp.arange(n_tok, dtype=jnp.int32), TOP_K)
    flat_w = top_w.reshape(-1)
    sorted_e, order = lax.sort((flat_e, jnp.arange(n_assign, dtype=jnp.int32)), num_keys=1, is_stable=True)
    counts = jnp.bincount(flat_e, length=N_EXPERTS)
    padded = (counts + EXPERT_BLOCK - 1) // EXPERT_BLOCK * EXPERT_BLOCK
    padded_end = jnp.cumsum(padded)
    padded_start = padded_end - padded
    start = jnp.cumsum(counts) - counts
    dest = padded_start[sorted_e] + jnp.arange(n_assign, dtype=jnp.int32) - start[sorted_e]
    n_blocks = -(-n_assign // EXPERT_BLOCK) + N_EXPERTS
    n_rows = n_blocks * EXPERT_BLOCK
    row_tok = jnp.full((n_rows,), n_tok, jnp.int32).at[dest].set(flat_tok[order])
    row_w = jnp.zeros((n_rows,), jnp.float32).at[dest].set(flat_w[order])
    block_e = jnp.minimum(jnp.searchsorted(padded_end, jnp.arange(n_blocks, dtype=jnp.int32) * EXPERT_BLOCK,
                                           side='right'), N_EXPERTS - 1)
    h_pad = jnp.concatenate([h, jnp.zeros((1, d), h.dtype)], axis=0)
    xs = h_pad[row_tok].reshape(n_blocks, EXPERT_BLOCK, d)

    def expert_block(args):
        xb, e = args
        hid = xb @ w_up[e] + b_up[e]
        return clamped_swiglu(hid) @ w_down[e] + b_down[e]

    ys = lax.map(expert_block, (xs, block_e)).reshape(n_rows, d)
    out = jnp.zeros((n_tok + 1, d), h.dtype).at[row_tok].add(ys * row_w[:, None].astype(h.dtype))
    return out[:n_tok]

def setup_inputs(seed: int = 0) -> dict:
    key = jax.random.key(seed)
    ks = jax.random.split(key, 24)

    def nrm(k, shape, scale):
        return scale * jax.random.normal(k, shape, jnp.float32)

    dt = jnp.exp(jax.random.uniform(ks[5], (DEPTH, H_DELTA), jnp.float32, math.log(1e-3), math.log(1e-1)))
    return {
        'x': nrm(ks[0], (BATCH, SEQ, D_MODEL), 1.0),
        'g_mix': 1.0 + nrm(ks[1], (DEPTH, D_MODEL), 0.02),
        'w_in': nrm(ks[2], (DEPTH, D_MODEL, D_IN), D_MODEL ** -0.5),
        'b_gate': nrm(ks[3], (DEPTH, 2, D_MODEL), 0.1),
        'conv_w': nrm(ks[4], (DEPTH, CONV_WIDTH, CONV_CH), CONV_WIDTH ** -0.5),
        'a_log': jnp.log(jax.random.uniform(ks[6], (DEPTH, H_DELTA), jnp.float32, 1.0, 16.0)),
        'dt_bias': dt + jnp.log(-jnp.expm1(-dt)),
        'g_delta_out': 1.0 + nrm(ks[7], (DEPTH, DV_DELTA), 0.02),
        'q_norm': 1.0 + nrm(ks[8], (DEPTH, DH_DIFF), 0.02),
        'k_norm': 1.0 + nrm(ks[9], (DEPTH, DH_DIFF), 0.02),
        'lambda_q1': nrm(ks[10], (DEPTH, DH_DIFF), 0.1),
        'lambda_k1': nrm(ks[11], (DEPTH, DH_DIFF), 0.1),
        'lambda_q2': nrm(ks[12], (DEPTH, DH_DIFF), 0.1),
        'lambda_k2': nrm(ks[13], (DEPTH, DH_DIFF), 0.1),
        'g_subln': 1.0 + nrm(ks[14], (DEPTH, DV_DIFF), 0.02),
        'rel_bias': nrm(ks[15], (N_BUCKETS, H_DIFF), 0.5),
        'w_o': nrm(ks[16], (DEPTH, D_MODEL, D_MODEL), D_MODEL ** -0.5),
        'g_ffn': 1.0 + nrm(ks[17], (DEPTH, D_MODEL), 0.02),
        'w_router': nrm(ks[18], (DEPTH, D_MODEL, N_EXPERTS), D_MODEL ** -0.5),
        'b_router': nrm(ks[19], (DEPTH, N_EXPERTS), 0.01),
        'w_up': nrm(ks[20], (DEPTH, N_EXPERTS, D_MODEL, 2 * D_FF), D_MODEL ** -0.5),
        'b_up': nrm(ks[21], (DEPTH, N_EXPERTS, 2 * D_FF), 0.02),
        'w_down': nrm(ks[22], (DEPTH, N_EXPERTS, D_FF, D_MODEL), D_FF ** -0.5),
        'b_down': nrm(ks[23], (DEPTH, N_EXPERTS, D_MODEL), 0.02),
    }

def reference(x, g_mix, w_in, b_gate, conv_w, a_log, dt_bias, g_delta_out, q_norm, k_norm,
              lambda_q1, lambda_k1, lambda_q2, lambda_k2, g_subln, rel_bias, w_o, g_ffn,
              w_router, b_router, w_up, b_up, w_down, b_down):
    bsz, seq, d = x.shape
    split_points = np.cumsum(IN_SPLITS)[:-1].tolist()
    for l in range(DEPTH):
        h = rms_norm(x, g_mix[l])
        proj = h @ w_in[l]
        (qa, ka, va, za, beta_in, a_in, qd, kd, vd, gate_a, gate_b) = jnp.split(proj, split_points, axis=-1)

        qkv = jax.nn.silu(causal_depthwise_conv(jnp.concatenate([qa, ka, va], axis=-1), conv_w[l]))
        qa, ka, va = jnp.split(qkv, [W_DELTA_QK, 2 * W_DELTA_QK], axis=-1)
        qa = l2_normalize(qa.reshape(bsz, seq, H_DELTA, DK_DELTA)) * (DK_DELTA ** -0.5)
        ka = l2_normalize(ka.reshape(bsz, seq, H_DELTA, DK_DELTA))
        va = va.reshape(bsz, seq, H_DELTA, DV_DELTA)
        beta = jax.nn.sigmoid(beta_in.astype(jnp.float32))
        g = -jnp.exp(a_log[l].astype(jnp.float32)) * jax.nn.softplus(
            a_in.astype(jnp.float32) + dt_bias[l].astype(jnp.float32))
        oa = gated_delta_rule(qa, ka, va, beta, g)
        oa = rms_norm(oa, g_delta_out[l]) * jax.nn.silu(za.reshape(bsz, seq, H_DELTA, DV_DELTA).astype(jnp.float32))
        oa = oa.reshape(bsz, seq, W_DELTA_V).astype(x.dtype)

        qd = rms_norm(qd.reshape(bsz, seq, H_DIFF, 2, DH_DIFF), q_norm[l])
        kd = rms_norm(kd.reshape(bsz, seq, H_DIFF, 2, DH_DIFF), k_norm[l])
        vd = vd.reshape(bsz, seq, H_DIFF, DV_DIFF)
        lam_init = 0.8 - 0.6 * math.exp(-0.3 * l)
        lam = (jnp.exp(jnp.sum(lambda_q1[l].astype(jnp.float32) * lambda_k1[l].astype(jnp.float32)))
               - jnp.exp(jnp.sum(lambda_q2[l].astype(jnp.float32) * lambda_k2[l].astype(jnp.float32)))
               + lam_init)
        od = diff_attention(qd, kd, vd, lam, rel_bias)
        od = (rms_norm(od, g_subln[l]) * (1.0 - lam_init)).reshape(bsz, seq, W_DIFF_V).astype(x.dtype)

        mix = jax.nn.sigmoid(gate_a + b_gate[l, 0]) * oa + jax.nn.sigmoid(gate_b + b_gate[l, 1]) * od
        x = x + mix @ w_o[l]

        h2 = rms_norm(x, g_ffn[l]).reshape(bsz * seq, d)
        x = x + moe_ffn(h2, w_router[l], b_router[l], w_up[l], b_up[l], w_down[l], b_down[l]).reshape(bsz, seq, d)
    return x


_drawn_inputs = setup_inputs


def setup_inputs(seed=0):
    import zlib

    import numpy as np

    out = dict(_drawn_inputs(seed))
    spreads = {}
    factors = {'lambda_q1': 5.385, 'b_up': 5.65, 'b_down': 6.483, 'g_delta_out': 3.145}
    for name, (base, spread) in spreads.items():
        noise = np.random.default_rng([zlib.crc32(name.encode()), seed]).standard_normal(out[name].shape)
        drawn = base * np.exp(spread * noise) if base else spread * noise
        out[name] = __import__('jax').numpy.asarray(drawn.astype(out[name].dtype))
    for name, factor in factors.items():
        out[name] = (out[name] * factor).astype(out[name].dtype)
    return out
```

```python
import math
from contextlib import ExitStack

import concourse.bass as bass
import numpy as np
from concourse import mybir

F32 = mybir.dt.float32
BF16 = mybir.dt.bfloat16
I32 = mybir.dt.int32
U32 = mybir.dt.uint32
ALU = mybir.AluOpType
ACT = mybir.ActivationFunctionType
AX_X = mybir.AxisListType.X

P = 128
EPS = 1e-6
LAM_INIT = 0.8 - 0.6 * math.exp(-0.3 * 0)
LIMIT = 7.0
ALPHA = 1.702
MAX_DISTANCE = 128
TOP_K = 4
SLOTS = 64
FUTURE = -1e30


def bucket_ranges(n_buckets, seq):
    exact = n_buckets // 2
    n = np.arange(seq)
    nf = np.maximum(n, 1).astype(np.float32)
    far = exact + (np.log(nf / exact) / math.log(MAX_DISTANCE / exact) * (n_buckets - exact)).astype(np.int32)
    b = np.where(n < exact, n, np.minimum(far, n_buckets - 1))
    return [(int(n[b == i].min()), int(n[b == i].max())) for i in range(n_buckets)]


def block_kernel(nc, x, g_mix, w_in, b_gate, conv_w, a_log, dt_bias, g_delta_out, q_norm, k_norm,
                 lambda_q1, lambda_k1, lambda_q2, lambda_k2, g_subln, rel_bias, w_o, g_ffn,
                 w_router, b_router, w_up, b_up, w_down, b_down, out):
    _, T, D = x.shape
    NB = T // P
    KC = D // P
    H = D // P
    E = w_router.shape[2]
    F = w_down.shape[2]
    NBUCK = rel_bias.shape[0]
    assert NB == 2 and KC == 8 and F == D and E == 32

    C_Q, C_K, C_V, C_Z, C_BA = 0, D, 2 * D, 3 * D, 4 * D
    C_QD = 4 * D + 2 * H
    C_KD, C_VD, C_GA, C_GB = C_QD + D, C_QD + 2 * D, C_QD + 3 * D, C_QD + 4 * D
    GROUPS = [("k", C_K), ("q", C_Q), ("v", C_V), ("qd", C_QD), ("kd", C_KD), ("vd", C_VD),
              ("z", C_Z), ("ga", C_GA), ("gb", C_GB)]
    NT = 8 * len(GROUPS)
    NPIECE = NT // 4
    places = [n % 4 for n in range(NPIECE)] + [4, 5]

    gdn = []
    for b in range(NB):
        gdn += [("gr", b), ("g1", b), ("g2", b), ("g2t", b)]
        for lv in range(3):
            gdn += [("sq", b, lv), ("upd", b, lv)]
        for m in range(2):
            gdn += [("m1", b, m), ("m2", b, m)]
        gdn += [("f1", b), ("f2", b)]
        gdn += [("o1", b), ("o2", b)] + ([("o3", b)] if b else [])
    attn = []
    for i in range(H + 3):
        attn += [(f"a{j + 1}", i - j) for j in range(4) if 0 <= i - j < H]
    sched = []
    extra = {10: [("nr", 0)], 12: [("nd", 0, 0)], 13: [("nd", 0, 1)], 16: [("ba",)], 18: [("nr", 1)], 19: [("gc",)],
             20: [("nd", 1, 0)], 21: [("nd", 1, 1)]}
    for t in range(24):
        sched.append(("tile", t))
        if 3 <= t < 19:
            sched.append(("nsum", t - 3))
        sched += extra.get(t, [])
    fill = [[("tile", 24)]] + [[("tile", t), ("nsum", t - 1)] + ([("nr", 2)] if t == 32 else []) for t in range(25, 40)]
    fill += [[("vd", 0), ("nsum", 39), ("nr", 3)]] + [[("vd", g)] for g in range(1, 4)]
    late = [("tile", t) for t in range(48, 72)]
    free = gdn.index(("g2t", 1))
    for i, g in enumerate(gdn):
        sched.append(g)
        if fill and i not in (4, 9, 14):
            sched += fill.pop(0)
        elif i > free and not fill and len(late) > 18:
            sched.append(late.pop(0))
    last, late = late[-2:], late[:-2]
    for s_ in [("nd", 3, 0), ("nd", 3, 1)] + [("on", h) for h in range(H)] + [("nr", 4), ("nd", 4, 0), ("nd", 4, 1), ("t5",)]:
        sched.append(s_)
        if late and (s_[0] == "nr" or s_[0] == "nd" or s_ == ("on", 3)):
            sched.append(late.pop(0))
    for i, s_ in enumerate(attn):
        sched.append(s_)
        if i % 2 and late:
            sched.append(late.pop(0))
    sched += [("nr", 5)] + late + last + [("nd", 5, 0), ("nd", 5, 1)]
    pe_sched = list(sched)
    for i in range(len(sched) - 1, 0, -1):
        if pe_sched[i][0] == "tile" and pe_sched[i - 1][0] in ("nd", "gc", "a4"):
            pe_sched[i - 1], pe_sched[i] = pe_sched[i], pe_sched[i - 1]
    half_no = {it: i for i, it in enumerate([i for i in sched if i[0] in ("tile", "vd")])}
    norm_no = {it: i for i, it in enumerate([i for i in sched if i[0] in ("nsum", "on")])}
    nr_no = {it: i + 1 for i, it in enumerate([i for i in sched if i[0] == "nr"])}
    MAPS = {0: 1, 1: 1, 2: 2, 3: 2, 4: 1, 5: 1}

    USES = {"gr": "A", "g1": "AB", "g2": "AB", "g2t": "A", "sq": "AB", "upd": "AB", "m1": "AB", "m2": "AB",
            "f1": "A", "f2": "A", "nd": "A", "t5": "AB"}
    O_USES = {("o1", 0): "A", ("o2", 0): "AB", ("o1", 1): "A", ("o2", 1): "B", ("o3", 1): "A"}
    nA, nB, a_, b_ = {}, {}, 0, 0
    for it in sched:
        use = USES.get(it[0]) or O_USES.get(it, "")
        if "A" in use:
            nA[it] = a_
            a_ += 1
        if "B" in use:
            nB[it] = b_
            b_ += 1
    GA, GB = nA[("o3", 1)] + 1, nB[("o2", 1)] + 1
    nds = [i for i in sched if i[0] == "nd"]

    ctx = ExitStack()
    with ctx:
        ctx.enter_context(nc.allow_non_contiguous_dma(reason="small parameter vectors"))

        def sb(name, shape, dt=F32):
            return ctx.enter_context(nc.sbuf_tensor(name, shape, dt))

        def sem(name):
            return ctx.enter_context(nc.semaphore(name))

        ring = sb("ring", [P, 12, 2 * D])
        xt = sb("xt", [P, NB, D])
        ra = sb("ra", [P, NB * D])
        hT = sb("hT", [P, KC, T])
        cT = sb("cT", [P, 3 * H, T])
        kn = sb("kn", [P, 2 * D])
        vb = sb("vb", [P, H, P])
        dl = sb("dl", [P, H * P])
        qk = sb("qk", [P, NB, H, P])
        qdec = sb("qdec", [P, H, P])
        atq = sb("atq", [P, H, T])
        atk = sb("atk", [P, H, T])
        atv = sb("atv", [P, NB, D])
        consts = sb("consts", [P, 13, P])
        ident, ones, tri, tri_s, low_s, bd64, nbd16, m32, m64, m128, map0, map1, flip = (consts[:, i, :] for i in range(13))
        par_rows = sb("par_rows", [P, P])
        par = sb("par", [P, P])
        par2 = sb("par2", [P, 40])
        wba = sb("wba", [P, KC, 2 * H])
        sm = sb("sm", [P, 520])
        rowbuf = sb("rowbuf", [8, 416])

        xn = ra[:, :].rearrange("p (b d) -> p b d", b=NB)
        A_ = ra[:, 0:D].rearrange("p (h j) -> p h j", h=H)
        X_ = ra[:, D:2 * D].rearrange("p (h j) -> p h j", h=H)
        kT, qT, vT = cT[:, 0:H, :], cT[:, H:2 * H, :], cT[:, 2 * H:3 * H, :]
        mats = ring[:, 8:12, :].rearrange("p s (m h j) -> p (s m) h j", m=2, h=H)
        Pm, Qm = [mats[:, 0], mats[:, 1]], [mats[:, 2], mats[:, 3]]
        S_, T_, AE, XE = mats[:, 4], mats[:, 5], mats[:, 6], mats[:, 7]
        kend = kn[:, 0:D].rearrange("p (h d) -> p h d", h=H)
        nkbg = kn[:, D:2 * D].rearrange("p (h d) -> p h d", h=H)
        state = kend
        VN0, WT, VN1 = Pm[0], Pm[1], Qm[0]
        oT, zg, gb_ = qT, vT, kT
        bias5 = kn[:, :].rearrange("p (h k) -> p h k", h=H)
        decl = dl[:, :].rearrange("p (h j) -> p h j", h=H)
        acc = [atv[:, 0, 0:256], atv[:, 0, 256:512]]
        sg = [atv[:, 0, 512:768], atv[:, 0, 768:1024]]
        sqb = sb("sqb", [P, 2, T])
        rn = sb("rn", [P, T])
        zb = sb("zb", [P, 2, T])
        conv_c = par[:, 0:96].rearrange("p (w t) -> p w t", w=4)
        gmix_c, gffn_c, bga_c, bgb_c = par2[:, 0:8], par2[:, 8:16], par2[:, 16:24], par2[:, 24:32]
        gdo_c, gsub_c, qn_c, kn_c = (par2[:, 32 + i:33 + i] for i in range(4))
        dv = [vb[:, :, :], dl[:, :].rearrange("p (h j) -> p h j", h=H)]

        pb = ctx.enter_context(nc.psum_tensor("pb", [P, 8, 512], F32))

        def half(i):
            return pb[:, i % 2, 0:T]

        psA = pb[:, 2:4, :].rearrange("p b (h j) -> p (b h) j", h=4)
        psB = pb[:, 4:6, :].rearrange("p b (h j) -> p (b h) j", h=4)
        psA_f = pb[:, 2:4, :].rearrange("p b j -> p (b j)")
        psB_f = pb[:, 4:6, :].rearrange("p b j -> p (b j)")

        lgt = [qk[:, :, :, :].rearrange("p b h j -> p (b h j)")[:, i * 768:(i + 1) * 768]
               .rearrange("p (m k) -> p m k", m=2) for i in range(2)]
        ex = dl[:, 0:768].rearrange("p (m k) -> p m k", m=2)
        aw = [qdec[:, :, :].rearrange("p h j -> p (h j)")[:, i * 384:(i + 1) * 384] for i in range(2)]
        aT = [vb[:, :, :].rearrange("p h j -> p (h j)")[:, i * 384:(i + 1) * 384]
              .rearrange("p (k q) -> p k q", k=3) for i in range(2)]
        r_dram = nc.dram_tensor("t5_rows", [8, 384], F32)

        def small(i, n=16):
            return sm[:, i:i + n]

        ba_a = small(16).rearrange("p (b h) -> p b h", b=2)
        beta = small(32).rearrange("p (b h) -> p b h", b=2)
        t1 = small(48).rearrange("p (b h) -> p b h", b=2)
        t2 = small(64).rearrange("p (b h) -> p b h", b=2)
        gg = small(80).rearrange("p (b h) -> p b h", b=2)
        gc = small(96).rearrange("p (b h) -> p b h", b=2)
        egc = small(112).rearrange("p (b h) -> p b h", b=2)
        kdec = small(136, 8)
        nbg = small(144, 8)
        dtb = small(152, 8)
        alog = small(160, 8)
        ss = small(168, 2)
        rr = small(170, 2)
        lamv = small(172, 4)
        lamc = small(176, 2)
        mx = small(178, 4)
        nmx = small(182, 4)
        es = small(186, 4)
        ers = small(190, 4)
        maxc = small(194, 1)
        nrnd = small(195, 1)
        rt2 = small(196, 2)
        rv, rt = small(200, 32), small(232, 32)

        def rs(g):
            return small(264 + 32 * g, 16 * MAPS[g])

        lamrow = sb("lamrow", [P, 4, 64])
        nr_i = sb("nr_i", [1, 2], I32)

        moe = atq[:, :, :].rearrange("p h t -> p (h t)")
        moe2 = atk[:, :, :].rearrange("p h t -> p (h t)")
        moe3 = atv[:, :, :].rearrange("p b d -> p (b d)")
        xg = moe[:, 0:512].rearrange("p (c s) -> p c s", c=8)
        glu, lin = moe[:, 512:1024], moe[:, 1024:1536]
        sgm = moe[:, 1536:2048]
        act = moe2[:, 0:512]
        actT = moe2[:, 512:1024].rearrange("p (j h s) -> p j h s", j=4, h=2)
        ys = moe2[:, 1024:1536]
        GT = moe2[:, 1536:1792]
        selg = moe2[:, 1792:2048].rearrange("p (b s) -> p b s", b=2)
        sel = moe3[:, 0:128].rearrange("p (b s) -> p b s", b=2)
        posm = moe3[:, 128:128 + 320].rearrange("p (b c) -> p b c", b=2)
        gate4 = moe3[:, 448:448 + 320].rearrange("p (b c) -> p b c", b=2)
        iota_s = moe3[:, 768:896]
        iota_e = moe3[:, 896:928]
        lg = moe3[:, 928:992].rearrange("p (b e) -> p b e", b=2)
        cho = moe3[:, 992:1056].rearrange("p (b e) -> p b e", b=2)
        gat = moe3[:, 1056:1120].rearrange("p (b e) -> p b e", b=2)
        top8 = moe3[:, 1120:1136].rearrange("p (b e) -> p b e", b=2)
        idx8 = moe3[:, 1136:1152].rearrange("p (b e) -> p b e", b=2)
        idxf = moe3[:, 1152:1168].rearrange("p (b e) -> p b e", b=2)
        wtop = moe3[:, 1168:1176].rearrange("p (b e) -> p b e", b=2)
        oneh = moe3[:, 1176:1208]
        brow = moe3[:, 1240:1272]
        s4 = moe3[:, 1272:1274]
        t4 = moe3[:, 1274:1276]
        gatT = moe3[:, 1276:1532].rearrange("p (b t) -> p b t", b=2)
        seleye = sb("seleye", [96, 160], BF16)
        selE = sb("selE", [96, SLOTS], BF16)
        ctf = cT[:, :, :].rearrange("p c t -> p (c t)")
        bup_f = ctf[0:96, 0:2048]
        bup_t = ctf[0:96, 2048:3072].bitcast(BF16)
        bup3 = ctf[0:96, 3072:4096].bitcast(BF16)
        bdn = ctf[0:32, 4096:5120]
        wrt = ctf[:, 5120:5376].rearrange("p (c e) -> p c e", c=8)
        idx_u = idx8.bitcast(U32)

        s_x, s_par, s_wba, s_small = sem("x_loaded"), sem("params_loaded"), sem("wba_loaded"), sem("small_loaded")
        s_piece = [sem(f"w_piece_loaded_{i}") for i in range(6)]
        s_used = sem("w_pieces_used")
        s_pool, s_dve, s_act = sem("pool_chain"), sem("dve_chain"), sem("act_chain")
        s_ident = sem("identity_built")
        s_const, s_t5st, s_t5 = sem("constants_built"), sem("t5_row_stored"), sem("t5_bias_loaded")
        s_ss, s_xn, s_tr, s_hT = sem("row_squares"), sem("rows_normalised"), sem("transposes_done"), sem("hT_blocks_ready")
        s_ptr, s_parc = sem("params_transposed"), sem("params_ready")
        s_pj, s_pjf = sem("proj_halves_done"), sem("proj_halves_taken")
        s_conv, s_sig, s_silu = sem("conv_done"), sem("conv_sigmoid_done"), sem("silu_done")
        s_sq, s_nmm = sem("norm_squares_ready"), sem("norm_sums_done")
        s_bap, s_bact, s_bdve = sem("beta_a_projected"), sem("beta_a_act_steps"), sem("beta_a_dve_steps")
        s_gcp, s_gc = sem("gc_summed"), sem("gc_ready")
        s_ug, s_dif, s_dex, s_dm, s_eg = sem("g_spread"), sem("g_difference"), sem("decay_exp"), sem("decay_masked"), sem("exp_gc_rows")
        s_psA, s_psAf = sem("psA_steps_done"), sem("psA_steps_taken")
        s_psB, s_psBf = sem("psB_steps_done"), sem("psB_steps_taken")
        s_spread = sem("roots_spread")
        s_var, s_root = sem("variance_ready"), sem("inverse_root_ready")
        s_E, s_qd = sem("merge_blocks_ready"), sem("qdec_ready")
        s_lam = sem("lambda_ready")
        s_lg, s_nm, s_ex = sem("logits_done"), sem("row_max_ready"), sem("exp_done")
        s_aw, s_atr, s_aT = sem("attn_weights_ready"), sem("attn_transposed"), sem("attnT_ready")
        s_od, s_ode, s_odn = sem("attn_output_done"), sem("attn_output_taken"), sem("attn_norm_summed")
        s_gate = sem("gates_applied")
        s_mix, s_wo, s_x1 = sem("mix_ready"), sem("w_o_product_done"), sem("x1_ready")
        s_lr, s_top, s_tex, s_cho = sem("router_logits_done"), sem("top_values_ready"), sem("top_exp_done"), sem("choice_ready")
        s_cs, s_plan, s_gtt, s_gtc = sem("positions_summed"), sem("route_plan_ready"), sem("gates_transposed"), sem("gatesT_ready")
        s_ml, s_bup = sem("moe_params_loaded"), sem("b_up_loaded")
        s_slab = [sem(f"slab_loaded_{i}") for i in range(12)]
        s_sused = sem("slabs_used")
        s_sel, s_sele, s_selg = sem("token_selection_ready"), sem("bias_selection_ready"), sem("gate_selection_ready")
        s_gath, s_xg, s_up, s_glu, s_lin = sem("tokens_gathered"), sem("tokens_ready"), sem("up_done"), sem("glu_ready"), sem("lin_ready")
        s_sgm, s_actv, s_actr, s_actT = sem("swiglu_sigmoid_done"), sem("act_ready"), sem("act_transposed"), sem("actT_ready")
        s_dn, s_ys, s_gtr, s_GT, s_comb = sem("down_done"), sem("ys_ready"), sem("gate_selection_transposed"), sem("GT_ready"), sem("expert_combined")
        s_mdve = sem("moe_dve_chain")
        s_fin, s_res, s_out = sem("all_experts_summed"), sem("result_ready"), sem("result_stored")

        block = ctx.enter_context(nc.Block())
        win = w_in[0]

        def w_piece(n):
            if n < NPIECE:
                c = GROUPS[n // 2][1] + 512 * (n % 2)
                return win[:, c:c + 512].rearrange("(k p) n -> p k n", p=P)
            return w_o[0][:, 512 * (n - NPIECE):512 * (n - NPIECE) + 512].rearrange("(k p) n -> p k n", p=P)

        def piece_at(n):
            s = 2 * places[n]
            return ring[:, s:s + 2, :].rearrange("p s (k n) -> p (s k) n", n=512)

        def piece_count(n):
            return 16 * places[:n + 1].count(places[n])

        @block.sync
        def _(sp):
            def slab(e, j):
                if j < 8:
                    src = w_up[0, e] if isinstance(e, int) else w_up[0, bass.ds(e, 1)].rearrange("a p n -> (a p) n")
                    return src[j * P:(j + 1) * P, :]
                src = w_down[0, e] if isinstance(e, int) else w_down[0, bass.ds(e, 1)].rearrange("a p n -> (a p) n")
                return src[(j - 8) * 2 * P:(j - 7) * 2 * P, :].rearrange("(c p) n -> p c n", p=P)

            def slot(j):
                return ring[:, j, :] if j < 8 else ring[:, j, :].rearrange("p (c n) -> p c n", c=2)

            def slot_free(k, j):
                if j == 7:
                    sp.wait_ge(s_up, k)
                elif j == 11:
                    sp.wait_ge(s_dn, k)
                else:
                    sp.wait_ge(s_sused, k * 10 + (j - 9 - j // 8))

            sp.dma_start(xt[:, :, :], x[0].rearrange("(b p) d -> p b d", p=P)).then_inc(s_x, 16)
            for n in range(NPIECE + 2):
                prev = [m for m in range(n) if places[m] == places[n]]
                if prev:
                    sp.wait_ge(s_used, prev[-1] + 1)
                if n == NPIECE:
                    sp.wait_ge(s_psAf, GA)
                    sp.wait_ge(s_psBf, GB)
                sp.dma_start(piece_at(n), w_piece(n)).then_inc(s_piece[places[n]], 16)
                if n == 1:
                    sp.dma_start(dtb, dt_bias[0:1, :].to_broadcast([P, H])).then_inc(s_small, 16)
                    sp.dma_start(alog, a_log[0:1, :].to_broadcast([P, H])).then_inc(s_small, 16)
                    for i, src in enumerate((lambda_q1, lambda_k1, lambda_q2, lambda_k2)):
                        sp.dma_start(lamrow[:, i, :], src[0:1, :].to_broadcast([P, 64])).then_inc(s_small, 16)
                    sp.dma_start(rowbuf[:, 384:384 + NBUCK], rel_bias.rearrange("b h -> h b")).then_inc(s_small, 16)
                    sp.dma_start(wba[:, :, :], win[:, C_BA:C_BA + 2 * H].rearrange("(k p) n -> p k n", p=P)).then_inc(s_wba, 16)
            for j in range(12):
                if j % 2 == 0:
                    sp.wait_ge(s_used, 1 + max(m for m in range(NPIECE + 2) if places[m] == j // 2))
                sp.dma_start(slot(j), slab(0, j)).then_inc(s_slab[j], 16)
            with sp.Fori(1, E) as e:
                for j in range(12):
                    slot_free(e, j)
                    sp.dma_start(slot(j), slab(e, j)).then_inc(s_slab[j], 16)
            sp.wait_ge(s_plan, 1)
            nr = sp.value_load(nr_i[0:1, 0:1], min_val=1, max_val=T // SLOTS)
            with sp.If(nr > 1):
                with sp.Fori(1, nr) as r:
                    with sp.Fori(0, E) as e:
                        for j in range(12):
                            slot_free(r * E + e, j)
                            sp.dma_start(slot(j), slab(e, j)).then_inc(s_slab[j], 16)
            for b in range(NB):
                sp.wait_ge(s_res, b + 1)
                sp.dma_start(out[0, b * P:(b + 1) * P, :], xt[:, b, :]).then_inc(s_out, 16)
            sp.wait_ge(s_out, 16 * NB)

        @block.gpsimd
        def _(pool):
            n = [0]

            def link(ins):
                n[0] += 1
                ins.then_inc(s_pool, 1)
                pool.wait_ge(s_pool, n[0])

            link(pool.memset(ident, 0.0))
            pool.affine_select(out=ident, in_=ident, compare_op=ALU.not_equal, fill=1.0, base=0, pattern=[[-1, P]], channel_multiplier=1).then_inc(s_ident, 1)
            pool.wait_ge(s_ident, 1)
            pool.memset(flip, 0.0)
            for m in (ones, tri, tri_s, low_s):
                pool.memset(m, 1.0)
            pool.memset(map0[:, 0:64], 1.0)
            pool.memset(map0[:, 64:P], 0.0)
            pool.memset(map1[:, 0:64], 0.0)
            pool.memset(map1[:, 64:P], 1.0)
            link(pool.memset(m128, 1.0))
            pool.affine_select(out=flip, in_=flip, compare_op=ALU.not_equal, fill=1.0, base=1 - P, pattern=[[1, P]], channel_multiplier=1)
            pool.affine_select(out=tri, in_=tri, compare_op=ALU.is_ge, fill=0.0, base=0, pattern=[[1, P]], channel_multiplier=-1)
            pool.affine_select(out=tri_s, in_=tri_s, compare_op=ALU.is_gt, fill=0.0, base=0, pattern=[[1, P]], channel_multiplier=-1)
            pool.affine_select(out=low_s, in_=low_s, compare_op=ALU.is_gt, fill=0.0, base=0, pattern=[[-1, P]], channel_multiplier=1)
            for m, w in ((nbd16, 16), (m32, 32), (bd64, 64)):
                v = m.rearrange("p (b w) -> p b w", w=w)
                o = m128.rearrange("p (b w) -> p b w", w=w)
                link(pool.affine_select(out=v, in_=o, compare_op=ALU.is_ge, fill=0.0, base=0, pattern=[[-w, P // w], [0, w]], channel_multiplier=1))
                link(pool.affine_select(out=v, in_=v, compare_op=ALU.is_ge, fill=0.0, base=w - 1, pattern=[[w, P // w], [0, w]], channel_multiplier=-1))
            link(pool.tensor_tensor(m64, bd64, m32, ALU.subtract))
            link(pool.tensor_tensor(m32, m32, nbd16, ALU.subtract))
            link(pool.tensor_tensor(m128, m128, bd64, ALU.subtract))
            link(pool.tensor_scalar(nbd16, nbd16, -1.0, None, ALU.mult))
            link(pool.memset(seleye[:, :], 0.0))
            for i in range(3):
                v = seleye[32 * i:32 * i + 32, :].rearrange("p (r e) -> p r e", e=32)
                link(pool.affine_select(out=v, in_=v, compare_op=ALU.not_equal, fill=1.0, base=0, pattern=[[0, 5], [-1, 32]], channel_multiplier=1))
            pool.sem_inc(s_const, 1)
            pool.wait_ge(s_small, 16 * 7)
            pool.memset(rowbuf[:, T:384], FUTURE)
            for i, (lo, hi) in enumerate(bucket_ranges(NBUCK, T)):
                ins = pool.tensor_copy(rowbuf[:, T - 1 - hi:T - lo], rowbuf[:, 384 + i:385 + i].to_broadcast([8, hi - lo + 1]))
            link(ins)
            pool.dma_start(r_dram.ap(), rowbuf[:, 0:384]).then_inc(s_t5st, 16)

            spread = lambda m: m[:, None, :].to_broadcast([P, H, P])
            for it in sched:
                if it == ("on", 0):
                    pool.wait_ge(s_t5st, 16)
                    pool.wait_ge(s_psAf, GA)
                    for h in range(H):
                        pool.dma_start(bias5[:, h, :], bass.AP(r_dram, h * 384, [[1, P], [1, T]])).then_inc(s_t5, 16)
                if it[0] == "gr":
                    b = it[1]
                    pool.wait_ge(s_dex, 2 * b + 2)
                    pool.tensor_tensor(decl, decl, spread(low_s), ALU.mult).then_inc(s_dm, 1)
                    pool.tensor_tensor(qk[:, b], qk[:, b], spread(tri), ALU.mult).then_inc(s_dm, 1)
                if it[0] == "g1" and it[1] == 1:
                    pool.wait_ge(s_eg, 1)
                    pool.tensor_tensor(qdec[:, :, :], qdec[:, :, :], qT[:, :, P:T], ALU.mult).then_inc(s_qd, 1)
                if it[0] == "g2":
                    b = it[1]
                    pool.wait_ge(s_psAf, nA[it] + 1)
                    link(pool.tensor_tensor(Pm[0], X_, spread(nbd16), ALU.mult))
                    link(pool.tensor_tensor(Qm[0], A_, spread(nbd16), ALU.mult))
                    pool.tensor_tensor(S_, Pm[0], spread(ident), ALU.add)
                    pool.tensor_tensor(T_, Qm[0], spread(ident), ALU.add)
                    pool.tensor_tensor(AE, A_, spread(m32), ALU.mult)
                    pool.tensor_tensor(XE, X_, spread(m32), ALU.mult).then_inc(s_E, 1)
                if it[0] == "m1":
                    _, b, m = it
                    pool.wait_ge(s_psA, nA[it] + 1)
                    pool.wait_ge(s_psB, nB[it] + 1)
                    nxt = (m64, m128)[m]
                    pool.tensor_tensor(AE, A_, spread(nxt), ALU.mult)
                    pool.tensor_tensor(XE, X_, spread(nxt), ALU.mult).then_inc(s_E, 1)
            pool.wait_ge(s_mix, H)
            for i in range(3):
                pool.dma_start(ctf[32 * i:32 * i + 32, 0:2048], b_up[0]).then_inc(s_bup, 16)
            pool.dma_start(bdn, b_down[0]).then_inc(s_ml, 16)
            pool.dma_start(wrt, w_router[0].rearrange("(c p) e -> p c e", p=P)).then_inc(s_ml, 16)
            pool.dma_start(brow, b_router[0:1, :].to_broadcast([P, E])).then_inc(s_ml, 16)
            pool.iota(iota_s, [[0, 2], [1, SLOTS]], base=0, channel_multiplier=0, allow_small_or_imprecise_dtypes=True)
            pool.iota(iota_e, [[1, E]], base=0, channel_multiplier=0, allow_small_or_imprecise_dtypes=True).then_inc(s_const, 1)

        @block.scalar
        def _(act_e):
            sc = nc.scalar

            def row_squares(dst):
                for b in range(NB):
                    sc.activation(dst[:, b, :], xt[:, b, :], ACT.Square, accum_out=ss[:, b:b + 1]).then_inc(s_ss, 1)

            act_e.dma_start(par_rows[0:96, :], conv_w[0].rearrange("w (t p) -> (w t) p", p=P)).then_inc(s_par, 16)
            rows2 = rn[0:36, 0:P]
            for at, src in ((0, g_mix), (8, g_ffn)):
                act_e.dma_start(rows2[at:at + 8, :], src[0:1].rearrange("a (t p) -> (a t) p", p=P)).then_inc(s_par, 16)
            act_e.dma_start(rows2[16:32, :], b_gate[0].rearrange("g (t p) -> (g t) p", p=P)).then_inc(s_par, 16)
            act_e.dma_start(rows2[32:33, :], g_delta_out[0:1, :]).then_inc(s_par, 16)
            act_e.dma_start(rows2[33:34, :], g_subln[0:1, :]).then_inc(s_par, 16)
            for i, src in enumerate((q_norm, k_norm)):
                for m in range(2):
                    act_e.dma_start(rows2[34 + i:35 + i, 64 * m:64 * m + 64], src[0:1, :]).then_inc(s_par, 16)
            act_e.wait_ge(s_x, 16)
            row_squares(xn)
            def root(i, a, of):
                act_e.wait_ge(s_var, i + 1)
                sc.activation(a, of, ACT.Sqrt).then_inc(s_root, 1)

            root(0, rr, rt2)
            act_e.wait_ge(s_small, 16 * 7)
            sc.activation(alog, alog, ACT.Exp).then_inc(s_bact, 1)
            act_e.wait_ge(s_lam, 1)
            sc.activation(lamv[:, 0:2], lamv[:, 0:2], ACT.Exp).then_inc(s_lam, 1)

            def take_tile(t):
                act_e.wait_ge(s_pj, half_no[("tile", t)] + 1)
                src = half(half_no[("tile", t)])
                if t < 24:
                    sc.copy(cT[:, t, :], src).then_inc(s_pjf, 1)
                    if t >= 1:
                        conv_sigmoid(t - 1)
                    if 2 <= t < 18:
                        square(("nsum", t - 2), cT[:, t - 2, :])
                elif t < 40:
                    if t == 24:
                        conv_sigmoid(23)
                    square(("nsum", t), src)
                    sc.copy((atq if t < 32 else atk)[:, t % 8, :], src).then_inc(s_pjf, 1)
                else:
                    h, g = t % 8, (t - 48) // 8
                    if g == 2:
                        if h == 0:
                            act_e.wait_ge(s_psB, nB[("g2", 1)] + 1)
                        sc.activation(gb_[:, h, :], src, ACT.Sigmoid, bias=bgb_c[:, h:h + 1]).then_inc(s_pjf, 1)
                        return
                    if g == 0 and h == 0:
                        act_e.wait_ge(s_psA, nA[("g2t", 1)] + 1)
                    i = 8 * g + h
                    if i >= 2:
                        act_e.wait_ge(s_gate, i - 1)
                    if g == 0:
                        sc.activation(zb[:, i % 2, :], src, ACT.Sigmoid)
                        sc.copy(zg[:, h, :], src).then_inc(s_pjf, 1)
                    else:
                        sc.activation(zb[:, i % 2, :], src, ACT.Sigmoid, bias=bga_c[:, h:h + 1]).then_inc(s_pjf, 1)

            def conv_sigmoid(t):
                act_e.wait_ge(s_conv, t + 1)
                if t >= 2:
                    act_e.wait_ge(s_silu, t - 1)
                sc.activation(sg[t % 2], acc[t % 2], ACT.Sigmoid).then_inc(s_sig, 1)

            def square(key, src):
                i = norm_no[key]
                if key[0] == "nsum" and key[1] < 16:
                    act_e.wait_ge(s_silu, key[1] + 1)
                if i >= 2:
                    act_e.wait_ge(s_nmm, i - 1)
                sc.activation(sqb[:, i % 2, :], src, ACT.Square).then_inc(s_sq, 1)

            def takeA(it, dst, src=psA):
                act_e.wait_ge(s_psA, nA[it] + 1)
                sc.copy(dst, src).then_inc(s_psAf, 1)

            for it in sched:
                if it[0] == "tile":
                    take_tile(it[1])
                elif it[0] == "vd":
                    b, hf = it[1] % 2, it[1] // 2
                    n = half_no[it]
                    act_e.wait_ge(s_pj, n + 1)
                    act_e.wait_ge(s_silu, 24)
                    sc.copy(atv[:, b, 512 * hf:512 * hf + 512], pb[:, n % 2, :]).then_inc(s_pjf, 1)
                elif it[0] == "nr":
                    root(nr_no[it], rs(it[1]), rt[:, 0:16 * MAPS[it[1]]])
                elif it[0] == "ba":
                    act_e.wait_ge(s_bap, 1)
                    sc.activation(t1, pb[:, 6, 0:32].rearrange("p (b n) -> p b n", b=2)[:, :, 0:H], ACT.Exp, scale=-1.0).then_inc(s_bact, 1)
                    act_e.wait_ge(s_bdve, 1)
                    sc.activation(t2, t2, ACT.Exp, scale=-1.0).then_inc(s_act, 1)
                    act_e.wait_ge(s_act, 1)
                    sc.activation(t2, t2, ACT.Ln, bias=1.0).then_inc(s_bact, 1)
                elif it[0] == "gc":
                    act_e.wait_ge(s_gc, 1)
                    sc.activation(egc, gc, ACT.Exp).then_inc(s_bact, 1)
                elif it[0] == "gr":
                    b = it[1]
                    if b == 1:
                        act_e.wait_ge(s_psA, nA[it] + 1)
                        sc.activation(qdec[:, :, :], psA, ACT.Exp).then_inc(s_eg, 1)
                    else:
                        act_e.wait_ge(s_bdve, 2)
                        sc.activation(kdec, kdec, ACT.Exp).then_inc(s_bact, 1)
                    act_e.wait_ge(s_dif, b + 1)
                    sc.activation(decl, decl, ACT.Exp, scale=-1.0).then_inc(s_dex, 1)
                    sc.activation(qk[:, b], qk[:, b], ACT.Exp).then_inc(s_dex, 1)
                elif it[0] == "g2":
                    takeA(it, X_)
                elif it[0] == "sq":
                    takeA(it, Pm[(it[2] + 1) % 2])
                elif it[0] in ("m1", "f1"):
                    takeA(it, Pm[0])
                elif it == ("o1", 0):
                    takeA(it, VN0)
                elif it == ("o2", 0):
                    takeA(it, state)
                elif it == ("o1", 1):
                    takeA(it, WT)
                elif it[0] == "on":
                    act_e.wait_ge(s_psAf, GA)
                    act_e.wait_ge(s_psBf, GB)
                    square(it, oT[:, it[1], :])
                elif it[0] == "a1":
                    h = it[1]
                    act_e.wait_ge(s_nm, h + 1)
                    if h >= 1:
                        act_e.wait_ge(s_aw, h)
                    for i in range(2):
                        sc.activation(ex[:, i, 0:T], lgt[h % 2][:, i, 0:T], ACT.Exp, bias=nmx[:, i:i + 1], accum_out=es[:, i:i + 1])
                        last = sc.activation(ex[:, i, T:T + P], lgt[h % 2][:, i, T:T + P], ACT.Exp, bias=nmx[:, 2 + i:3 + i], accum_out=es[:, 2 + i:3 + i])
                    last.then_inc(s_ex, 1)
                elif it[0] == "a2":
                    h = it[1]
                    act_e.wait_ge(s_atr, h + 1)
                    if h >= 2:
                        act_e.wait_ge(s_od, h - 1)
                    sc.copy(aT[h % 2], pb[:, 6, 0:3 * P].rearrange("p (k q) -> p k q", k=3)).then_inc(s_aT, 1)
                elif it[0] == "a3":
                    h = it[1]
                    act_e.wait_ge(s_od, h + 1)
                    if h >= 2:
                        act_e.wait_ge(s_odn, h - 1)
                    else:
                        act_e.wait_ge(s_nmm, 40)
                    sc.activation(sqb[:, h % 2, :], pb[:, 7, 0:T], ACT.Square)
                    sc.copy(atq[:, h, :], pb[:, 7, 0:T]).then_inc(s_ode, 1)
            act_e.wait_ge(s_x1, NB)
            row_squares(xn)
            root(7, rr, rt2)
            for b in range(NB):
                act_e.wait_ge(s_top, b + 1)
                sc.activation(wtop[:, b, :], top8[:, b, 0:TOP_K], ACT.Exp, bias=t4[:, b:b + 1], accum_out=s4[:, b:b + 1]).then_inc(s_tex, 1)

            act_e.wait_ge(s_plan, 1)
            nr = act_e.value_load(nr_i[0:1, 0:1], min_val=1, max_val=T // SLOTS)
            with act_e.Fori(0, nr) as r:
                with act_e.Fori(0, E) as e:
                    n = r * E + e
                    act_e.wait_ge(s_glu, n + 2)
                    sc.activation(sgm, glu, ACT.Sigmoid, scale=ALPHA).then_inc(s_sgm, 1)
                    act_e.wait_ge(s_gtr, n + 1)
                    act_e.wait_ge(s_comb, n + 1)
                    sc.copy(GT, pb[:, 2, 0:T]).then_inc(s_GT, 1)
                    for j in range(2):
                        act_e.wait_ge(s_actr, 2 * n + j + 1)
                        sc.copy(moe2[:, 512 + 256 * j:768 + 256 * j], pb[:, j, 0:256]).then_inc(s_actT, 1)
                    act_e.wait_ge(s_dn, n + 1)
                    sc.copy(ys, pb[:, 2, :]).then_inc(s_ys, 1)

        @block.vector
        def _(dve):
            v = nc.vector
            n = [0]

            def link(ins):
                n[0] += 1
                ins.then_inc(s_dve, 1)
                dve.wait_ge(s_dve, n[0])

            def roots(i, y, x_, inv):
                v.reciprocal(inv, x_).then_inc(s_var, 1)
                dve.wait_ge(s_root, i + 1)
                link(v.tensor_tensor(inv, y, y, ALU.mult))
                link(v.tensor_tensor(x_, x_, inv, ALU.mult))
                link(v.tensor_scalar(x_, x_, -0.5, 1.5, ALU.mult, ALU.add))
                link(v.tensor_tensor(y, y, x_, ALU.mult))

            def rows_normalised(i, count):
                dve.wait_ge(s_ss, count)
                link(v.tensor_scalar(ss, ss, 1.0 / D, EPS, ALU.mult, ALU.add))
                roots(i, rr, ss, rt2)
                for b in range(NB):
                    v.tensor_scalar(xn[:, b, :], xt[:, b, :], rr[:, b:b + 1], None, ALU.mult).then_inc(s_xn, 1)

            def transposes_taken(gain, count0):
                for i in range(4):
                    b, c0 = i // 2, 4 * (i % 2)
                    dve.wait_ge(s_tr, count0 + i + 1)
                    v.tensor_tensor(hT[:, c0:c0 + 4, b * P:(b + 1) * P], pb[:, 2 + i, :].rearrange("p (c t) -> p c t", c=4),
                                    gain[:, c0:c0 + 4, None].to_broadcast([P, 4, P]), ALU.mult).then_inc(s_hT, 1)

            rows_normalised(0, NB)
            dve.wait_ge(s_ptr, 1)
            v.tensor_copy(par[:, 0:96], pb[:, 6, 0:96])
            link(v.tensor_copy(par2[:, 0:36], pb[:, 6, 128:164]))
            v.tensor_scalar(par2[:, 32:33], par2[:, 32:33], math.sqrt(P), None, ALU.mult)
            v.tensor_scalar(par2[:, 33:34], par2[:, 33:34], math.sqrt(P) * (1.0 - LAM_INIT), None, ALU.mult)
            v.scalar_tensor_tensor(out=qn_c, in0=qn_c, scalar=math.sqrt(64), in1=kn_c, op0=ALU.mult, op1=ALU.mult).then_inc(s_parc, 1)
            dve.wait_ge(s_parc, 1)
            transposes_taken(gmix_c, 0)
            dve.wait_ge(s_small, 16 * 7)
            link(v.tensor_tensor(lamrow[:, 0, :], lamrow[:, 0, :], lamrow[:, 1, :], ALU.mult))
            link(v.tensor_tensor(lamrow[:, 2, :], lamrow[:, 2, :], lamrow[:, 3, :], ALU.mult))
            v.tensor_reduce(lamv[:, 0:1], lamrow[:, 0, :], AX_X, ALU.add)
            v.tensor_reduce(lamv[:, 1:2], lamrow[:, 2, :], AX_X, ALU.add).then_inc(s_lam, 1)
            dve.wait_ge(s_lam, 2)
            link(v.tensor_tensor(lamc[:, 0:1], lamv[:, 1:2], lamv[:, 0:1], ALU.subtract))
            link(v.tensor_scalar(lamc[:, 0:1], lamc[:, 0:1], -LAM_INIT, None, ALU.add))

            def conv(t):
                dve.wait_ge(s_pjf, half_no[("tile", t)] + 1)
                if t >= 2:
                    dve.wait_ge(s_sig, t - 1)
                    dve.wait_ge(s_silu, t - 1)
                a, src = acc[t % 2], cT[:, t, :]
                tap = t ^ 8 if t < 16 else t
                link(v.tensor_scalar(a, src, conv_c[:, 3, tap:tap + 1], None, ALU.mult))
                for d in (1, 2, 3):
                    ins = v.scalar_tensor_tensor(out=a[:, d:], in0=src[:, 0:T - d], scalar=conv_c[:, 3 - d, tap:tap + 1], in1=a[:, d:], op0=ALU.mult, op1=ALU.add)
                    if d < 3:
                        link(ins)
                ins.then_inc(s_conv, 1)
                dve.wait_ge(s_conv, t + 1)

            def silu(t):
                dve.wait_ge(s_sig, t + 1)
                v.tensor_tensor(cT[:, t, :], acc[t % 2], sg[t % 2], ALU.mult).then_inc(s_silu, 1)

            def takeA(it):
                dve.wait_ge(s_psA, nA[it] + 1)

            def takeB(it):
                dve.wait_ge(s_psB, nB[it] + 1)

            def per_head(dst, src, col, done):
                for h in range(H):
                    ins = v.tensor_scalar(dst[:, h], src[:, h], col[:, h:h + 1], None, ALU.mult)
                ins.then_inc(done, 1)

            for it in sched:
                if it[0] == "tile":
                    t = it[1]
                    if t < 24:
                        conv(t)
                    if 1 <= t <= 24:
                        silu(t - 1)
                    if 48 <= t < 64:
                        i = t - 48
                        dve.wait_ge(s_pjf, half_no[it] + 1)
                        v.tensor_tensor(zg[:, i % 8, :], zg[:, i % 8, :], zb[:, i % 2, :], ALU.mult).then_inc(s_gate, 1)
                elif it[0] == "nr":
                    g = it[1]
                    c = 16 * MAPS[g]
                    dve.wait_ge(s_odn, H) if g == 5 else dve.wait_ge(s_nmm, 8 * (g + 1))
                    src = pb[:, 6, 384:384 + c] if g == 5 else pb[:, 7, 0:c]
                    eps = (1.0, 1.0, 64.0, 64.0, float(P), float(P))[g] * EPS
                    link(v.tensor_scalar(rv[:, 0:c], src, eps, None, ALU.add))
                    roots(nr_no[it], rs(g), rv[:, 0:c], rt[:, 0:c])
                elif it[0] == "nd":
                    _, g, b = it
                    i = nds.index(it)
                    if i:
                        dve.wait_ge(s_psA, nA[nds[i - 1]] + 1)
                    if g >= 3:
                        dve.wait_ge(s_psA, GA)
                    if g == 5:
                        dve.wait_ge(s_odn, H)
                    for m in range(MAPS[g]):
                        col = rs(g).rearrange("p (b h m) -> p b h m", b=NB, m=MAPS[g])[:, b, :, m:m + 1]
                        ins = v.tensor_tensor(dv[(m + (g >= 3)) % 2], ident[:, None, :].to_broadcast([P, H, P]), col.to_broadcast([P, H, P]), ALU.mult)
                    ins.then_inc(s_spread, 1)
                    takeA(it)
                    dst, gain = ((kT, 1.0), (qT, P ** -0.5), None, (atk, qn_c), (oT, gdo_c), (atq, gsub_c))[g]
                    if g == 5:
                        dve.wait_ge(s_ode, H)
                    if g == 3:
                        dve.wait_ge(s_pjf, half_no[("tile", 39)] + 1)
                    if g < 2:
                        dve.wait_ge(s_silu, 8 * g + 8)
                    blk = slice(b * P, (b + 1) * P)
                    v.scalar_tensor_tensor(out=dst[:, :, blk], in0=dst[:, :, blk], scalar=gain, in1=psA, op0=ALU.mult, op1=ALU.mult).then_inc(s_psAf, 1)
                elif it[0] == "ba":
                    dve.wait_ge(s_bact, 2)
                    link(v.tensor_scalar(beta, t1, 1.0, None, ALU.add))
                    link(v.reciprocal(beta, beta))
                    psa = pb[:, 6, 0:32].rearrange("p (b n) -> p b n", b=2)[:, :, H:2 * H]
                    link(v.tensor_tensor(ba_a, psa, dtb[:, None, :].to_broadcast([P, NB, H]), ALU.add))
                    v.scalar_tensor_tensor(out=t2, in0=ba_a, scalar=-1.0, in1=ba_a, op0=ALU.mult, op1=ALU.max).then_inc(s_bdve, 1)
                    dve.wait_ge(s_bact, 3)
                    link(v.scalar_tensor_tensor(out=gg, in0=ba_a, scalar=0.0, in1=t2, op0=ALU.max, op1=ALU.add))
                    v.scalar_tensor_tensor(out=gg, in0=gg, scalar=-1.0, in1=alog[:, None, :].to_broadcast([P, NB, H]), op0=ALU.mult, op1=ALU.mult).then_inc(s_ug, 1)
                elif it[0] == "gc":
                    dve.wait_ge(s_gcp, 1)
                    v.tensor_copy(gc, pb[:, 6, 64:80].rearrange("p (b h) -> p b h", b=2)).then_inc(s_gc, 1)
                    dve.wait_ge(s_bact, 4)
                    link(v.scalar_tensor_tensor(out=nbg, in0=beta[:, 1, :], scalar=-1.0, in1=egc[:, 1, :], op0=ALU.mult, op1=ALU.mult))
                elif it[0] == "gr":
                    b = it[1]
                    if not b:
                        dve.wait_ge(s_psA, nA[("nd", 1, 1)] + 1)
                    if b:
                        dve.wait_ge(s_psAf, nA[("o1", 0)] + 1)
                    v.tensor_tensor(vb[:, :, :], tri[:, None, :].to_broadcast([P, H, P]), gg[:, b, :, None].to_broadcast([P, H, P]), ALU.mult).then_inc(s_ug, 1)
                    takeA(it)
                    if b == 0:
                        v.tensor_tensor(kdec, psA[:, :, P - 1], gc[:, 0, :], ALU.subtract).then_inc(s_bdve, 1)
                        dve.wait_ge(s_gc, 1)
                    else:
                        dve.wait_ge(s_eg, 1)
                    if b:
                        dve.wait_ge(s_psAf, nA[("g1", 0)] + 1)
                    link(v.tensor_tensor(decl, psA, gc[:, b, :, None].to_broadcast([P, H, P]), ALU.subtract))
                    link(v.tensor_scalar(qk[:, b], decl, 0.0, None, ALU.min))
                    v.tensor_scalar(decl, decl, 0.0, None, ALU.max).then_inc(s_dif, 1)
                    dve.wait_ge(s_dif, b + 1)
                    dve.sem_inc(s_psAf, 1)
                elif it[0] == "g1":
                    b = it[1]
                    takeA(it)
                    dve.wait_ge(s_dm, 2 * b + 2)
                    for h in range(H):
                        ins = v.scalar_tensor_tensor(out=A_[:, h], in0=psA[:, h], scalar=beta[:, b, h:h + 1], in1=decl[:, h], op0=ALU.mult, op1=ALU.mult)
                    ins.then_inc(s_psAf, 1)
                    takeB(it)
                    v.tensor_tensor(qk[:, b], qk[:, b], psB, ALU.mult).then_inc(s_psBf, 1)
                elif it[0] == "g2":
                    b = it[1]
                    takeB(it)
                    if b == 0:
                        dve.wait_ge(s_bact, 5)
                    per_head(nkbg if b else kend, psB, nbg if b else kdec, s_psBf)
                elif it[0] == "g2t":
                    takeA(it)
                    per_head(vb, psA, beta[:, it[1], :], s_psAf)
                elif it[0] == "sq":
                    takeB(it)
                    v.tensor_copy(Qm[(it[2] + 1) % 2], psB).then_inc(s_psBf, 1)
                elif it[0] in ("upd", "m2"):
                    op = ALU.add if it[0] == "upd" else ALU.subtract
                    takeA(it)
                    takeB(it)
                    v.tensor_tensor(S_, S_, psA, op).then_inc(s_psAf, 1)
                    v.tensor_tensor(T_, T_, psB, op).then_inc(s_psBf, 1)
                elif it[0] == "m1":
                    takeB(it)
                    v.tensor_copy(Qm[0], psB).then_inc(s_psBf, 1)
                elif it[0] == "f2":
                    takeA(it)
                    v.tensor_tensor(S_, S_, psA, ALU.subtract).then_inc(s_psAf, 1)
                elif it == ("o2", 0):
                    takeB(it)
                    v.tensor_copy(oT[:, :, 0:P], psB).then_inc(s_psBf, 1)
                elif it == ("o2", 1):
                    takeB(it)
                    v.tensor_copy(VN1, psB).then_inc(s_psBf, 1)
                elif it == ("o3", 1):
                    takeA(it)
                    v.tensor_copy(oT[:, :, P:T], psA).then_inc(s_psAf, 1)
                elif it[0] == "t5":
                    takeA(it)
                    takeB(it)
                    v.tensor_copy(kn[:, 0:D], psA_f).then_inc(s_psAf, 1)
                    v.tensor_copy(kn[:, D:2 * D], psB_f).then_inc(s_psBf, 1)
                elif it[0] == "a1":
                    h = it[1]
                    dve.wait_ge(s_lg, h + 1)
                    if h == 0:
                        dve.wait_ge(s_psBf, nB[("t5",)] + 1)
                    if h >= 2:
                        dve.wait_ge(s_ex, h - 1)
                    b0 = 2 + 2 * (h % 2)
                    rq = rs(2).rearrange("p (b h m) -> p b h m", b=NB, m=2)
                    for m in range(2):
                        v.scalar_tensor_tensor(out=lgt[h % 2][:, m, 0:T], in0=pb[:, b0 + m, 0:T], scalar=rq[:, 1, h, m:m + 1], in1=bias5[:, h, :], op0=ALU.mult, op1=ALU.add)
                        ins = v.scalar_tensor_tensor(out=lgt[h % 2][:, m, T:T + P], in0=pb[:, b0 + m, T:T + P], scalar=rq[:, 0, h, m:m + 1], in1=bias5[:, h, P:T], op0=ALU.mult, op1=ALU.add)
                    link(ins)
                    if h >= 1:
                        dve.wait_ge(s_nm, h)
                        dve.wait_ge(s_aw, h)
                    v.tensor_reduce(mx[:, 0:2], lgt[h % 2][:, :, 0:T], AX_X, ALU.max)
                    link(v.tensor_reduce(mx[:, 2:4], lgt[h % 2][:, :, T:T + P], AX_X, ALU.max))
                    v.tensor_scalar(nmx, mx, -1.0, None, ALU.mult).then_inc(s_nm, 1)
                    dve.wait_ge(s_ex, h + 1)
                    link(v.reciprocal(ers, es))
                    if h >= 2:
                        dve.wait_ge(s_atr, h - 1)
                    link(v.tensor_scalar(ers[:, 1:4:2], ers[:, 1:4:2], lamc[:, 0:1], None, ALU.mult))
                    for j, (lo, hi) in enumerate(((0, T), (T, T + P))):
                        link(v.tensor_scalar(aw[h % 2][:, lo:hi], ex[:, 0, lo:hi], ers[:, 2 * j:2 * j + 1], None, ALU.mult))
                        ins = v.scalar_tensor_tensor(out=aw[h % 2][:, lo:hi], in0=ex[:, 1, lo:hi], scalar=ers[:, 2 * j + 1:2 * j + 2], in1=aw[h % 2][:, lo:hi], op0=ALU.mult, op1=ALU.add)
                    ins.then_inc(s_aw, 1)
            dve.wait_ge(s_used, NPIECE)
            dve.wait_ge(s_pjf, max(half_no.values()) + 1)
            dve.wait_ge(s_gate, 16)
            dve.wait_ge(s_psAf, nA[("nd", 5, 1)] + 1)
            for h in range(H):
                v.tensor_tensor(oT[:, h, :], oT[:, h, :], zg[:, h, :], ALU.mult)
                link(v.tensor_tensor(atq[:, h, :], atq[:, h, :], gb_[:, h, :], ALU.mult))
                v.tensor_tensor(hT[:, h, :], oT[:, h, :], atq[:, h, :], ALU.add).then_inc(s_mix, 1)
            dve.wait_ge(s_mix, H)
            dve.wait_ge(s_bup, 16 * 3)
            for i in range(3):
                link(v.tensor_copy(bup_t, bup_f))
                link(v.tensor_copy(bup3[32 * i:32 * i + 32, :], bup_t[32 * i:32 * i + 32, :]))
                if i < 2:
                    link(v.tensor_tensor(bup_f, bup_f, bup_t, ALU.subtract))
            for b in range(NB):
                dve.wait_ge(s_wo, 2 * b + 2)
                v.tensor_tensor(xt[:, b, :], xt[:, b, :], pb[:, 2 + 2 * b:4 + 2 * b, :].rearrange("p n j -> p (n j)"), ALU.add).then_inc(s_x1, 1)
            dve.wait_ge(s_x1, NB)
            rows_normalised(7, 2 * NB)
            transposes_taken(gffn_c, 4)
            dve.wait_ge(s_ml, 16 * 3)
            dve.wait_ge(s_const, 2)
            dve.wait_ge(s_lr, 1)
            link(v.tensor_tensor(lg, pb[:, 6, 0:64].rearrange("p (b e) -> p b e", b=2), brow[:, None, :].to_broadcast([P, NB, E]), ALU.add))
            for b in range(NB):
                link(v.max(top8[:, b, :], lg[:, b, :]))
                v.tensor_scalar(t4[:, b:b + 1], top8[:, b, 0:1], -1.0, None, ALU.mult).then_inc(s_top, 1)
                link(v.max_index(idx_u[:, b, :], top8[:, b, :], lg[:, b, :]))
                link(v.tensor_copy(idxf[:, b, :], idx_u[:, b, :]))
                dve.wait_ge(s_tex, b + 1)
                link(v.reciprocal(s4[:, b:b + 1], s4[:, b:b + 1]))
                link(v.tensor_scalar(wtop[:, b, :], wtop[:, b, :], s4[:, b:b + 1], None, ALU.mult))
                link(v.tensor_scalar(gat[:, b, :], iota_e, idxf[:, b, 0:1], wtop[:, b, 0:1], ALU.is_equal, ALU.mult))
                for j in range(1, TOP_K):
                    link(v.tensor_scalar(oneh, iota_e, idxf[:, b, j:j + 1], wtop[:, b, j:j + 1], ALU.is_equal, ALU.mult))
                    link(v.tensor_tensor(gat[:, b, :], gat[:, b, :], oneh, ALU.add))
                v.tensor_scalar(cho[:, b, :], gat[:, b, :], 0.0, None, ALU.is_gt).then_inc(s_cho, 1)
            dve.wait_ge(s_cs, 1)
            pos = pb[:, 6, 64:128].rearrange("p (b e) -> p b e", b=2)
            link(v.scalar_tensor_tensor(out=lg, in0=pos, scalar=1.0, in1=cho, op0=ALU.add, op1=ALU.mult))
            v.memset(posm[:, :, P:160], -1.0)
            v.memset(gate4[:, :, P:160], 0.0)
            for r in range(T // SLOTS):
                v.tensor_scalar(posm[:, :, r * E:(r + 1) * E], lg, -1.0 - SLOTS * r, None, ALU.add)
                v.tensor_copy(gate4[:, :, r * E:(r + 1) * E], gat)
            link(v.tensor_reduce(maxc, pb[:, 6, 128:160], AX_X, ALU.max))
            link(v.tensor_scalar(nrnd, maxc, float(SLOTS), 1.0, ALU.is_gt, ALU.add))
            for r in range(2, T // SLOTS):
                link(v.scalar_tensor_tensor(out=nrnd, in0=maxc, scalar=float(SLOTS * r), in1=nrnd, op0=ALU.is_gt, op1=ALU.add))
            v.memset(ys, 0.0)
            v.memset(GT, 0.0)
            v.tensor_copy(nr_i[0:1, 0:1], nrnd[0:1, 0:1]).then_inc(s_plan, 1)
            dve.wait_ge(s_gtt, 1)
            v.tensor_copy(gatT[0:E, :, :], pb[0:E, 3, 0:256].rearrange("p (b t) -> p b t", b=2)).then_inc(s_gtc, 1)
            v.tensor_copy(selE[:, :], seleye[:, 0:1].to_broadcast([96, SLOTS])).then_inc(s_sele, 1)

            def select(col):
                for b in range(NB):
                    ins = v.tensor_scalar(sel[:, b, :], iota_s[:, 0:SLOTS], posm[:, b, col], None, ALU.is_equal)
                ins.then_inc(s_sel, 1)

            def take_gathered():
                v.tensor_tensor(xg, pb[:, 3, :].rearrange("p (c s) -> p c s", c=8),
                                gffn_c[:, :, None].to_broadcast([P, KC, SLOTS]), ALU.mult).then_inc(s_xg, 1)

            dve.wait_ge(s_plan, 1)
            for s_ in (s_GT, s_ys, s_glu, s_lin):
                dve.sem_inc(s_, 1)
            dve.sem_inc(s_actT, 2)
            select(slice(0, 1))
            dve.wait_ge(s_gath, 1)
            take_gathered()
            nr = dve.value_load(nr_i[0:1, 0:1], min_val=1, max_val=T // SLOTS)
            with dve.Fori(0, nr) as r:
                with dve.Fori(0, E) as e:
                    k = r * E + e
                    dve.wait_ge(s_gath, k + 1)
                    select(bass.ds(k + 1, 1))
                    dve.wait_ge(s_GT, k + 1)
                    for b in range(NB):
                        ins = v.tensor_scalar(selg[:, b, :], iota_s, posm[:, b, bass.ds(k, 1)], gate4[:, b, bass.ds(k, 1)], ALU.is_equal, ALU.mult)
                    ins.then_inc(s_selg, 1)
                    dve.wait_ge(s_up, k + 1)
                    pairs = pb[:, 0:2, :].rearrange("p n (f two) -> p n f two", two=2)
                    g2, l2 = glu.rearrange("p (n f) -> p n f", n=2), lin.rearrange("p (n f) -> p n f", n=2)
                    v.tensor_scalar(g2, pairs[:, :, :, 0], LIMIT, None, ALU.min).then_inc(s_glu, 1)
                    v.tensor_scalar(l2, pairs[:, :, :, 1], LIMIT, -LIMIT, ALU.min, ALU.max).then_inc(s_lin, 1)
                    dve.wait_ge(s_sgm, k + 1)
                    v.tensor_tensor(sgm, sgm, glu, ALU.mult).then_inc(s_mdve, 1)
                    dve.wait_ge(s_mdve, k + 1)
                    dve.wait_ge(s_lin, k + 2)
                    v.scalar_tensor_tensor(out=act, in0=lin, scalar=1.0, in1=sgm, op0=ALU.add, op1=ALU.mult).then_inc(s_actv, 1)
                    v.tensor_copy(selE[:, :], seleye[:, bass.ds(k + 1, 1)].to_broadcast([96, SLOTS])).then_inc(s_sele, 1)
                    dve.wait_ge(s_gath, k + 2)
                    take_gathered()
            dve.wait_ge(s_fin, 1)
            for b in range(NB):
                v.tensor_tensor(xt[:, b, :], xt[:, b, :], pb[:, 4 + 2 * b:6 + 2 * b, :].rearrange("p n j -> p (n j)"), ALU.add).then_inc(s_res, 1)

        @block.tensor
        def _(pe):
            mm = nc.tensor.matmul

            def transposes(count_ready):
                for i in range(4):
                    b, c0 = i // 2, 4 * (i % 2)
                    pe.wait_ge(s_xn, count_ready + b + 1)
                    for c in range(4):
                        ins = nc.tensor.transpose(pb[:, 2 + i, c * P:(c + 1) * P], xn[:, b, (c0 + c) * P:(c0 + c + 1) * P], ident)
                    ins.then_inc(s_tr, 1)

            pe.wait_ge(s_ident, 1)
            pe.wait_ge(s_par, 16 * 10)
            nc.tensor.transpose(pb[:, 6, 0:96], par_rows[0:96, :], ident[0:96, 0:96])
            nc.tensor.transpose(pb[:, 6, 128:164], rn[0:36, 0:P], ident[0:36, 0:36]).then_inc(s_ptr, 1)
            transposes(0)
            pe.wait_ge(s_hT, 4)
            pe.wait_ge(s_parc, 1)
            pe.wait_ge(s_const, 1)

            def half_free(n):
                if n >= 2:
                    pe.wait_ge(s_pjf, n - 1)

            def startA(it):
                pe.wait_ge(s_psAf, nA[it])

            def startB(it):
                pe.wait_ge(s_psBf, nB[it])

            def heads(ps, lhs, rhs, start=True, stop=True):
                for h in range(H):
                    ins = mm(ps[:, h], lhs(h), rhs(h), start=start, stop=stop)
                return ins

            for it in pe_sched:
                if it[0] == "tile":
                    t = it[1]
                    n, hn = t // 4, half_no[it]
                    half_free(hn)
                    pe.wait_ge(s_piece[places[n]], piece_count(n))
                    w = piece_at(n)
                    for c in range(KC):
                        ins = mm(half(hn), w[:, c, (t % 4) * P:(t % 4) * P + P], hT[:, c, :], start=(c == 0), stop=(c == KC - 1))
                    ins.then_inc(s_pj, 1)
                    if t % 4 == 3:
                        pe.wait_ge(s_pj, hn + 1)
                        pe.sem_inc(s_used, 1)
                elif it[0] == "vd":
                    g = it[1]
                    b, hf, hn = g % 2, g // 2, half_no[it]
                    half_free(hn)
                    n = 10 + hf
                    pe.wait_ge(s_piece[places[n]], piece_count(n))
                    bank = hn % 2
                    for c in range(KC):
                        ins = mm(pb[:, bank, :], hT[:, c, b * P:(b + 1) * P], piece_at(n)[:, c, :], start=(c == 0), stop=(c == KC - 1))
                    ins.then_inc(s_pj, 1)
                    if b == 1:
                        pe.wait_ge(s_pj, hn + 1)
                        pe.sem_inc(s_used, 1)
                elif it[0] in ("nsum", "on"):
                    i = norm_no[it]
                    g = i // 8
                    pe.wait_ge(s_sq, i + 1)
                    if i % 8 == 0 and g:
                        pe.wait_ge(s_var, g + 1)
                    for b in range(NB):
                        c = (b * H + i % 8) * MAPS[g]
                        cols = ones[:, 0:1] if MAPS[g] == 1 else bd64[:, 0:P:64]
                        ins = mm(pb[:, 7, c:c + MAPS[g]], sqb[:, i % 2, b * P:(b + 1) * P], cols, start=True, stop=True)
                    ins.then_inc(s_nmm, 1)
                elif it[0] == "nd":
                    g = it[1]
                    startA(it)
                    pe.wait_ge(s_spread, nds.index(it) + 1)
                    for i in range(2):
                        flat = [d[:, 4 * i:4 * i + 4, :].rearrange("p h j -> p (h j)") for d in dv]
                        if MAPS[g] == 2:
                            mm(pb[:, 2 + i, :], map0, flat[1], start=True, stop=False)
                            ins = mm(pb[:, 2 + i, :], map1, flat[0], start=False, stop=True)
                        else:
                            ins = mm(pb[:, 2 + i, :], ones, flat[g >= 3], start=True, stop=True)
                    ins.then_inc(s_psA, 1)
                elif it[0] == "ba":
                    pe.wait_ge(s_wba, 16)
                    for b in range(NB):
                        for c in range(KC):
                            ins = mm(pb[:, 6, 16 * b:16 * b + 16], hT[:, c, b * P:(b + 1) * P], wba[:, c, :], start=(c == 0), stop=(c == KC - 1))
                    ins.then_inc(s_bap, 1)
                elif it[0] == "gc":
                    pe.wait_ge(s_ug, 1)
                    for b in range(NB):
                        ins = mm(pb[:, 6, 64 + 8 * b:72 + 8 * b], tri, gg[:, b, :], start=True, stop=True)
                    ins.then_inc(s_gcp, 1)
                elif it[0] == "gr":
                    startA(it)
                    pe.wait_ge(s_ug, 2 + it[1])
                    for i in range(2):
                        ins = mm(pb[:, 2 + i, :], ones, vb[:, 4 * i:4 * i + 4, :].rearrange("p h j -> p (h j)"), start=True, stop=True)
                    ins.then_inc(s_psA, 1)
                elif it[0] == "g1":
                    b = it[1]
                    startA(it)
                    blk = slice(b * P, (b + 1) * P)
                    heads(psA, lambda h: kT[:, h, blk], lambda h: kT[:, h, blk]).then_inc(s_psA, 1)
                    startB(it)
                    heads(psB, lambda h: kT[:, h, blk], lambda h: qT[:, h, blk]).then_inc(s_psB, 1)
                elif it[0] == "g2":
                    b = it[1]
                    blk = slice(b * P, (b + 1) * P)
                    startA(it)
                    for h in range(H):
                        ins = nc.tensor.transpose(psA[:, h], A_[:, h], ident)
                    ins.then_inc(s_psA, 1)
                    startB(it)
                    for h in range(H):
                        ins = nc.tensor.transpose(psB[:, h], kT[:, h, blk], ident)
                    ins.then_inc(s_psB, 1)
                elif it[0] == "g2t":
                    blk = slice(it[1] * P, (it[1] + 1) * P)
                    startA(it)
                    pe.wait_ge(s_silu, 24)
                    for h in range(H):
                        ins = nc.tensor.transpose(psA[:, h], vT[:, h, blk], ident)
                    ins.then_inc(s_psA, 1)
                elif it[0] == "sq":
                    _, b, lv = it
                    p, q = Pm[lv % 2], Qm[lv % 2]
                    startA(it)
                    startB(it)
                    if lv == 0:
                        pe.wait_ge(s_E, 3 * b + 1)
                    heads(psA, lambda h: q[:, h], lambda h: p[:, h]).then_inc(s_psA, 1)
                    heads(psB, lambda h: p[:, h], lambda h: q[:, h]).then_inc(s_psB, 1)
                elif it[0] == "upd":
                    _, b, lv = it
                    p, q = Pm[(lv + 1) % 2], Qm[(lv + 1) % 2]
                    startA(it)
                    startB(it)
                    heads(psA, lambda h: q[:, h], lambda h: S_[:, h]).then_inc(s_psA, 1)
                    heads(psB, lambda h: p[:, h], lambda h: T_[:, h]).then_inc(s_psB, 1)
                elif it[0] == "m1":
                    _, b, m = it
                    startA(it)
                    startB(it)
                    pe.wait_ge(s_E, 3 * b + m + 1)
                    heads(psA, lambda h: AE[:, h], lambda h: S_[:, h]).then_inc(s_psA, 1)
                    heads(psB, lambda h: XE[:, h], lambda h: T_[:, h]).then_inc(s_psB, 1)
                elif it[0] == "m2":
                    startA(it)
                    startB(it)
                    heads(psA, lambda h: T_[:, h], lambda h: Pm[0][:, h]).then_inc(s_psA, 1)
                    heads(psB, lambda h: S_[:, h], lambda h: Qm[0][:, h]).then_inc(s_psB, 1)
                elif it[0] == "f1":
                    startA(it)
                    pe.wait_ge(s_psBf, nB[("m2", it[1], 1)] + 1)
                    pe.wait_ge(s_E, 3 * it[1] + 3)
                    heads(psA, lambda h: AE[:, h], lambda h: S_[:, h]).then_inc(s_psA, 1)
                elif it[0] == "f2":
                    startA(it)
                    heads(psA, lambda h: T_[:, h], lambda h: Pm[0][:, h]).then_inc(s_psA, 1)
                elif it == ("o1", 0):
                    startA(it)
                    heads(psA, lambda h: S_[:, h], lambda h: vb[:, h]).then_inc(s_psA, 1)
                elif it == ("o2", 0):
                    startA(it)
                    startB(it)
                    heads(psA, lambda h: kend[:, h], lambda h: VN0[:, h]).then_inc(s_psA, 1)
                    heads(psB, lambda h: VN0[:, h], lambda h: qk[:, 0, h]).then_inc(s_psB, 1)
                elif it == ("o1", 1):
                    startA(it)
                    heads(psA, lambda h: nkbg[:, h], lambda h: S_[:, h]).then_inc(s_psA, 1)
                elif it == ("o2", 1):
                    startB(it)
                    pe.wait_ge(s_psAf, nA[("o1", 1)] + 1)
                    for h in range(H):
                        mm(psB[:, h], S_[:, h], vb[:, h], start=True, stop=False)
                        ins = mm(psB[:, h], WT[:, h], state[:, h], start=False, stop=True)
                    ins.then_inc(s_psB, 1)
                elif it == ("o3", 1):
                    startA(it)
                    pe.wait_ge(s_qd, 1)
                    pe.wait_ge(s_psBf, nB[("o2", 1)] + 1)
                    for h in range(H):
                        mm(psA[:, h], state[:, h], qdec[:, h], start=True, stop=False)
                        ins = mm(psA[:, h], VN1[:, h], qk[:, 1, h], start=False, stop=True)
                    ins.then_inc(s_psA, 1)
                elif it[0] == "t5":
                    startA(it)
                    startB(it)
                    pe.wait_ge(s_t5, 16 * H)
                    for i in range(4):
                        ins = mm(pb[:, 2 + i, :], flip, kn[:, 512 * i:512 * i + 512], start=True, stop=True)
                        if i % 2:
                            ins.then_inc((s_psA, s_psB)[i // 2], 1)
                elif it[0] == "a1":
                    h = it[1]
                    b0 = 2 + 2 * (h % 2)
                    if h == 0:
                        pe.wait_ge(s_psAf, nA[("t5",)] + 1)
                        pe.wait_ge(s_psBf, nB[("t5",)] + 1)
                    if h >= 2:
                        pe.wait_ge(s_nm, h - 1)
                    for m in range(2):
                        rows = slice(64 * m, 64 * m + 64)
                        mm(pb[:, b0 + m, 0:T], atq[rows, h, P:T], atk[rows, h, :], start=True, stop=True)
                        ins = mm(pb[:, b0 + m, T:T + P], atq[rows, h, 0:P], atk[rows, h, 0:P], start=True, stop=True)
                    ins.then_inc(s_lg, 1)
                elif it[0] == "a2":
                    h = it[1]
                    pe.wait_ge(s_aw, h + 1)
                    if h >= 1:
                        pe.wait_ge(s_aT, h)
                    for k in range(3):
                        ins = nc.tensor.transpose(pb[:, 6, k * P:(k + 1) * P], aw[h % 2][:, k * P:(k + 1) * P], ident)
                    ins.then_inc(s_atr, 1)
                elif it[0] == "a3":
                    h = it[1]
                    pe.wait_ge(s_aT, h + 1)
                    if h == 0:
                        pe.wait_ge(s_var, 6)
                        pe.wait_ge(s_pjf, half_no[("vd", 3)] + 1)
                    if h >= 1:
                        pe.wait_ge(s_ode, h)
                    val = [atv[:, k, h * P:(h + 1) * P] for k in range(2)]
                    mm(pb[:, 7, P:T], val[0], aT[h % 2][:, 0], start=True, stop=False)
                    mm(pb[:, 7, P:T], val[1], aT[h % 2][:, 1], start=False, stop=True)
                    mm(pb[:, 7, 0:P], val[0], aT[h % 2][:, 2], start=True, stop=True).then_inc(s_od, 1)
                elif it[0] == "a4":
                    h = it[1]
                    pe.wait_ge(s_ode, h + 1)
                    pe.wait_ge(s_aT, min(h + 3, H))
                    for b in range(NB):
                        ins = mm(pb[:, 6, 384 + b * H + h:385 + b * H + h], sqb[:, h % 2, b * P:(b + 1) * P], ones[:, 0:1], start=True, stop=True)
                    ins.then_inc(s_odn, 1)
            for n in range(2):
                pe.wait_ge(s_piece[places[NPIECE + n]], piece_count(NPIECE + n))
            for b in range(NB):
                for n in range(2):
                    for c in range(KC):
                        if b == 0 and n == 0:
                            pe.wait_ge(s_mix, c + 1)
                        ins = mm(pb[:, 2 + 2 * b + n, :], hT[:, c, b * P:(b + 1) * P], piece_at(NPIECE + n)[:, c, :], start=(c == 0), stop=(c == KC - 1))
                    ins.then_inc(s_wo, 1)
            pe.wait_ge(s_wo, 2 * NB)
            pe.sem_inc(s_used, 2)
            pe.wait_ge(s_x1, NB)
            transposes(2)
            pe.wait_ge(s_hT, 8)
            pe.wait_ge(s_ml, 16 * 3)
            for b in range(NB):
                for c in range(KC):
                    ins = mm(pb[:, 6, E * b:E * b + E], hT[:, c, b * P:(b + 1) * P], wrt[:, c, :], start=(c == 0), stop=(c == KC - 1))
            ins.then_inc(s_lr, 1)
            pe.wait_ge(s_cho, NB)
            mm(pb[:, 6, 64:96], tri_s, cho[:, 0, :], start=True, stop=True)
            mm(pb[:, 6, 96:128], ones, cho[:, 0, :], start=True, stop=False)
            mm(pb[:, 6, 96:128], tri_s, cho[:, 1, :], start=False, stop=True)
            mm(pb[:, 6, 128:160], ones, cho[:, 0, :], start=True, stop=False)
            mm(pb[:, 6, 128:160], ones, cho[:, 1, :], start=False, stop=True).then_inc(s_cs, 1)
            for b in range(NB):
                ins = nc.tensor.transpose(pb[0:E, 3, b * P:(b + 1) * P], gat[:, b, :], ident)
            ins.then_inc(s_gtt, 1)
            pe.wait_ge(s_gtc, 1)
            for b in range(NB):
                for n in range(2):
                    mm(pb[:, 4 + 2 * b + n, :], gatT[0:E, b, :], bdn[:, 512 * n:512 * n + 512], start=True, stop=True, skip_group_check=True)

            def gather():
                for c in range(KC):
                    for b in range(NB):
                        ins = mm(pb[:, 3, c * SLOTS:(c + 1) * SLOTS], xn[:, b, c * P:(c + 1) * P], sel[:, b, :], start=(b == 0), stop=(b == NB - 1))
                ins.then_inc(s_gath, 1)

            def combine():
                for b in range(NB):
                    for n in range(2):
                        rows = slice(64 * n, 64 * n + 64)
                        ins = mm(pb[:, 4 + 2 * b + n, :], GT[rows, b * P:(b + 1) * P], ys[rows, :], start=False, stop=True, skip_group_check=True)
                return ins

            pe.wait_ge(s_sel, 1)
            gather()
            nr = pe.value_load(nr_i[0:1, 0:1], min_val=1, max_val=T // SLOTS)
            with pe.Fori(0, nr) as r:
                with pe.Fori(0, E) as e:
                    k = r * E + e
                    pe.wait_ge(s_sele, k + 1)
                    pe.wait_ge(s_xg, k + 1)
                    pe.wait_ge(s_actT, 2 * k + 2)
                    for n in range(2):
                        for hf in range(2):
                            mm(pb[64 * hf:64 * hf + 64, n, :], selE[:, :], bup3[:, (2 * hf + n) * 512:(2 * hf + n + 1) * 512], start=True, stop=False, skip_group_check=True)
                    for c in range(KC):
                        pe.wait_ge(s_slab[c], k * 16 + 16)
                        for n in range(2):
                            for hf in range(2):
                                ins = mm(pb[64 * hf:64 * hf + 64, n, :], xg[:, c, :], ring[:, c, (2 * hf + n) * 512:(2 * hf + n + 1) * 512], start=False, stop=(c == KC - 1), skip_group_check=True)
                        if c < KC - 1:
                            ins.then_inc(s_sused, 1)
                        else:
                            ins.then_inc(s_up, 1)
                    pe.wait_ge(s_ys, k + 1)
                    pe.wait_ge(s_selg, k + 1)
                    for b in range(NB):
                        ins = nc.tensor.transpose(pb[:, 2, b * P:(b + 1) * P], selg[:, b, :], ident)
                    ins.then_inc(s_gtr, 1)
                    combine().then_inc(s_comb, 1)
                    pe.wait_ge(s_actv, k + 1)
                    for j in range(4):
                        ins = nc.tensor.transpose(pb[:, j // 2, (j % 2) * P:(j % 2 + 1) * P], act[:, j * P:(j + 1) * P], ident)
                        if j % 2:
                            ins.then_inc(s_actr, 1)
                    pe.wait_ge(s_sel, k + 2)
                    gather()
                    pe.wait_ge(s_GT, k + 2)
                    for c in range(KC):
                        j, hf_in = c % 4, c // 4
                        if c % 2 == 0:
                            if c < 4:
                                pe.wait_ge(s_actT, 2 * k + c // 2 + 3)
                            pe.wait_ge(s_slab[8 + c // 2], k * 16 + 16)
                        for hf in range(2):
                            ins = mm(pb[64 * hf:64 * hf + 64, 2, :], actT[:, j, hf_in, :], ring[:, 8 + c // 2, (c % 2) * 1024 + hf * 512:(c % 2) * 1024 + hf * 512 + 512], start=(c == 0), stop=(c == KC - 1), skip_group_check=True)
                        if c % 2 == 1 and c < KC - 1:
                            ins.then_inc(s_sused, 1)
                    ins.then_inc(s_dn, 1)
            pe.wait_ge(s_GT, nr * E + 1)
            pe.wait_ge(s_ys, nr * E + 1)
            combine().then_inc(s_fin, 1)


_INS = ["x", "g_mix", "w_in", "b_gate", "conv_w", "a_log", "dt_bias", "g_delta_out", "q_norm", "k_norm",
        "lambda_q1", "lambda_k1", "lambda_q2", "lambda_k2", "g_subln", "rel_bias", "w_o", "g_ffn",
        "w_router", "b_router", "w_up", "b_up", "w_down", "b_down"]


def kernel(**inputs):
    import concourse.bacc as bacc
    from concourse.bass_utils import run_bass_kernel_spmd

    nc = bacc.Bacc("TRN2", target_bir_lowering=False, num_devices=1, dynamic_dma_scratch_size=8192)
    arrays, args = {}, []
    for name in _INS:
        a = np.ascontiguousarray(inputs[name])
        arrays[f"in_{name}_dram"] = a
        args.append(nc.dram_tensor(f"in_{name}_dram", a.shape, mybir.dt.from_np(a.dtype), kind="ExternalInput").ap())
    o = nc.dram_tensor("out_dram", inputs["x"].shape, F32, kind="ExternalOutput").ap()
    block_kernel(nc, *args, o)
    r = run_bass_kernel_spmd(nc, [arrays], core_ids=[0])
    return r.results[0]["out_dram"]
```
